# Optimizing a Trainium2 kernel written in Bass

```python
import jax, jax.numpy as jnp
from jax import lax
import numpy as np

D_MODEL = 1024
BATCH = 1
SEQ = 512
DEPTH = 2

N_META = 16
EXPAND = 2
D_INNER = EXPAND * D_MODEL
N_A = DEPTH // 2
N_B = DEPTH - N_A
GLA_HEADS = 4
GLA_DK_TOTAL = D_INNER // 2
GLA_HEAD_K = GLA_DK_TOTAL // GLA_HEADS
GLA_HEAD_V = D_INNER // GLA_HEADS
GLA_GATE_RANK = 16
GLA_GATE_NORMALIZER = 16.0
GLA_CHUNK = 16
GLA_IN_COLS = 2 * GLA_DK_TOTAL + D_INNER + GLA_GATE_RANK + D_INNER
FOX_HEADS = 16
FOX_HEAD_DIM = D_INNER // FOX_HEADS
FOX_BLOCK = 128
FOX_IN_COLS = 2 * D_INNER
KV_COLS = 2 * D_INNER + FOX_HEADS
RMS_EPS = 1e-6
NEG_INF = -1e30

kernel_name = "gla_fox_yoco_meta_hybrid"

def rmsnorm(x, g):
    xf = x.astype(jnp.float32)
    y = xf * lax.rsqrt(jnp.mean(xf * xf, axis=-1, keepdims=True) + RMS_EPS)
    return (y * g.astype(jnp.float32)).astype(x.dtype)

def gla_chunked(q, k, v, log_a):
    B, L, H, dk = q.shape
    dv = v.shape[-1]
    n_chunks = L // GLA_CHUNK

    def to_chunks(t):
        return t.reshape(B, n_chunks, GLA_CHUNK, H, t.shape[-1]).transpose(1, 0, 3, 2, 4)

    qc, kc, vc, gc = to_chunks(q), to_chunks(k), to_chunks(v), to_chunks(log_a.astype(jnp.float32))
    causal = jnp.tril(jnp.ones((GLA_CHUNK, GLA_CHUNK), dtype=bool))

    def step(S, inp):
        qn, kn, vn, gn = inp
        b = jnp.cumsum(gn, axis=-2)
        b_last = b[..., -1:, :]
        q_dec = qn * jnp.exp(b)
        k_inv = kn * jnp.exp(-b)
        k_rem = kn * jnp.exp(b_last - b)
        attn = jnp.where(causal, jnp.einsum('bhik,bhjk->bhij', q_dec, k_inv), 0.0)
        o = jnp.einsum('bhij,bhjv->bhiv', attn, vn) + jnp.einsum('bhik,bhkv->bhiv', q_dec, S)
        S = jnp.exp(b_last[..., 0, :])[..., None] * S + jnp.einsum('bhjk,bhjv->bhkv', k_rem, vn)
        return S, o

    S0 = jnp.zeros((B, H, dk, dv), jnp.float32)
    _, o = lax.scan(step, S0, (qc, kc, vc, gc))
    return o.transpose(1, 0, 3, 2, 4).reshape(B, L, H, dv).astype(v.dtype)

def gla_layer(h, norm_g, w_in, w_gate_up, b_gate, head_norm_g, w_out):
    B, L, _ = h.shape
    proj = rmsnorm(h, norm_g) @ w_in
    o1 = GLA_DK_TOTAL
    o2 = 2 * GLA_DK_TOTAL
    o3 = o2 + D_INNER
    o4 = o3 + GLA_GATE_RANK
    q, k, v, g_low, r = jnp.split(proj, [o1, o2, o3, o4], axis=-1)
    log_a = jax.nn.log_sigmoid((g_low @ w_gate_up + b_gate).astype(jnp.float32)) / GLA_GATE_NORMALIZER
    q = q.reshape(B, L, GLA_HEADS, GLA_HEAD_K) * (GLA_HEAD_K ** -0.5)
    k = k.reshape(B, L, GLA_HEADS, GLA_HEAD_K)
    v = v.reshape(B, L, GLA_HEADS, GLA_HEAD_V)
    log_a = log_a.reshape(B, L, GLA_HEADS, GLA_HEAD_K)
    o = gla_chunked(q, k, v, log_a)
    o = rmsnorm(o, head_norm_g).reshape(B, L, D_INNER)
    return h + (o * jax.nn.silu(r)) @ w_out

def fox_shared_kv(h, kv_norm_g, w_kv, b_forget):
    B, L, _ = h.shape
    proj = rmsnorm(h, kv_norm_g) @ w_kv
    k, v, f_logit = jnp.split(proj, [D_INNER, 2 * D_INNER], axis=-1)
    k = k.reshape(B, L, FOX_HEADS, FOX_HEAD_DIM).transpose(0, 2, 1, 3)
    v = v.reshape(B, L, FOX_HEADS, FOX_HEAD_DIM).transpose(0, 2, 1, 3)
    log_f = jax.nn.log_sigmoid((f_logit + b_forget).astype(jnp.float32))
    cum = jnp.cumsum(log_f, axis=1).transpose(0, 2, 1)
    return k, v, cum

def fox_layer(h, norm_g, w_in, w_out, k, v, cum):
    B, L, _ = h.shape
    q, r = jnp.split(rmsnorm(h, norm_g) @ w_in, 2, axis=-1)
    q = q.reshape(B, L, FOX_HEADS, FOX_HEAD_DIM).transpose(0, 2, 1, 3) * (FOX_HEAD_DIM ** -0.5)
    bounds = [0, N_META] + list(range(N_META + FOX_BLOCK, L + 1, FOX_BLOCK))
    outs = []
    for start, end in zip(bounds[:-1], bounds[1:]):
        s = jnp.einsum('bhqd,bhkd->bhqk', q[:, :, start:end], k[:, :, :end]).astype(jnp.float32)
        s = s + cum[:, :, start:end, None] - cum[:, :, None, :end]
        causal = jnp.arange(start, end)[:, None] >= jnp.arange(end)[None, :]
        p = jax.nn.softmax(jnp.where(causal, s, NEG_INF), axis=-1)
        outs.append(jnp.einsum('bhqk,bhkd->bhqd', p.astype(v.dtype), v[:, :, :end]))
    o = jnp.concatenate(outs, axis=2).transpose(0, 2, 1, 3).reshape(B, L, D_INNER)
    return h + (o * jax.nn.silu(r)) @ w_out

def setup_inputs(seed: int = 0) -> dict:
    key = jax.random.key(seed)
    ks = jax.random.split(key, 16)
    f32 = jnp.float32
    nrm = lambda k, shape, scale: jax.random.normal(k, shape, f32) * scale
    return {
        "x": nrm(ks[0], (BATCH, SEQ, D_MODEL), 1.0),
        "meta_tokens": nrm(ks[1], (N_META, D_MODEL), 1.0),
        "norm_g": 1.0 + nrm(ks[2], (DEPTH, D_MODEL), 0.02),
        "gla_w_in": nrm(ks[3], (N_A, D_MODEL, GLA_IN_COLS), D_MODEL ** -0.5),
        "gla_w_gate_up": nrm(ks[4], (N_A, GLA_GATE_RANK, GLA_DK_TOTAL), GLA_GATE_RANK ** -0.5),
        "gla_b_gate": nrm(ks[5], (N_A, GLA_DK_TOTAL), 0.02),
        "gla_head_norm_g": 1.0 + nrm(ks[6], (N_A, GLA_HEAD_V), 0.02),
        "gla_w_out": nrm(ks[7], (N_A, D_INNER, D_MODEL), 0.5 * D_INNER ** -0.5),
        "kv_norm_g": 1.0 + nrm(ks[8], (D_MODEL,), 0.02),
        "fox_w_kv": nrm(ks[9], (D_MODEL, KV_COLS), D_MODEL ** -0.5),
        "fox_b_forget": nrm(ks[10], (FOX_HEADS,), 0.02),
        "fox_w_in": nrm(ks[11], (N_B, D_MODEL, FOX_IN_COLS), D_MODEL ** -0.5),
        "fox_w_out": nrm(ks[12], (N_B, D_INNER, D_MODEL), 0.5 * D_INNER ** -0.5),
        "final_norm_g": 1.0 + nrm(ks[13], (D_MODEL,), 0.02),
    }

def reference(x, meta_tokens, norm_g, gla_w_in, gla_w_gate_up, gla_b_gate, gla_head_norm_g,
              gla_w_out, kv_norm_g, fox_w_kv, fox_b_forget, fox_w_in, fox_w_out, final_norm_g):
    B = x.shape[0]
    meta = jnp.broadcast_to(meta_tokens[None].astype(x.dtype), (B, N_META, D_MODEL))
    h = jnp.concatenate([meta, x], axis=1)
    k_sh = v_sh = cum_sh = None
    for layer in range(DEPTH):
        if layer < N_A:
            h = gla_layer(h, norm_g[layer], gla_w_in[layer], gla_w_gate_up[layer], gla_b_gate[layer],
                          gla_head_norm_g[layer], gla_w_out[layer])
        else:
            if layer == N_A:
                k_sh, v_sh, cum_sh = fox_shared_kv(h, kv_norm_g, fox_w_kv, fox_b_forget)
            j = layer - N_A
            h = fox_layer(h, norm_g[layer], fox_w_in[j], fox_w_out[j], k_sh, v_sh, cum_sh)
    h = rmsnorm(h, final_norm_g)
    return h[:, N_META:]


_drawn_inputs = setup_inputs


def setup_inputs(seed=0):
    import zlib

    import numpy as np

    out = dict(_drawn_inputs(seed))
    spreads = {}
    factors = {'norm_g': 4.274,
     'gla_b_gate': 8.0,
     'gla_head_norm_g': 8.0,
     'kv_norm_g': 8.0,
     'fox_b_forget': 8.0,
     'final_norm_g': 2.746}
    for name, (base, spread) in spreads.items():
        noise = np.random.default_rng([zlib.crc32(name.encode()), seed]).standard_normal(out[name].shape)
        drawn = base * np.exp(spread * noise) if base else spread * noise
        out[name] = __import__('jax').numpy.asarray(drawn.astype(out[name].dtype))
    for name, factor in factors.items():
        out[name] = (out[name] * factor).astype(out[name].dtype)
    return out
```

```python
import concourse.bass as bass
from concourse import mybir
from contextlib import ExitStack

F32 = mybir.dt.float32
F32R = mybir.dt.float32r
I32 = mybir.dt.int32
ALU = mybir.AluOpType
ACT = mybir.ActivationFunctionType
AX = mybir.AxisListType

P = 128
D_MODEL = 1024
D_INNER = 2 * D_MODEL
META = 16
SEQ = 512
T = META + SEQ
HALF = T // 2
KT = D_MODEL // P
BLK = 128
NBLK = SEQ // BLK
GLA_HEADS = 4
GLA_DK, GLA_DV = D_INNER // 2 // GLA_HEADS, D_INNER // GLA_HEADS
CT, VT = GLA_DK // P, GLA_DV // P
GLA_Q_SCALE = GLA_DK ** -0.5
GATE_NORM = 16.0
RANK = 16
FOX_HEADS = 16
FOX_Q_SCALE = (D_INNER // FOX_HEADS) ** -0.5
PAIRS = FOX_HEADS // 2
EPS = 1e-6
BANK = 512
CH = 1024

GLA_CHUNKS = ["Q0", "Q1", "K0", "K1", "V0", "R0", "V1", "R1", "V2", "R2", "V3", "R3", "W0", "W2", "W4", "W6"]
FOX_CHUNKS = ["K0", "Q0", "V0", "R0", "K1", "Q1", "V1", "R1", "W0", "W4"]
GLA_RING, FOX_RING = 4, 5
AHEAD = 2
GLA_JOBS = ["G0", "G1", "Q0", "Q1", "K0", "K1", "V0", "R0", "X0", "V1", "R1", "X1", "V2", "A0", "R2", "A1", "X2",
            "V3", "A2", "X3", "R3", "A3"] + [f"W{d}" for d in range(KT)]
FOX_JOBS = ["K0", "Q0", "V0", "R0", "X0", "K1", "Q1", "A0", "V1", "X1", "R1", "A1"] + [f"W{d}" for d in range(KT)]

PK = [0, 512, 1024, 1408, 1664]
PK_W = [512, 512, 384, 256, 128]
PK_META = 1792
PK_ALL = PK_META + META

C_IDENT, C_BELOW, C_NEG, C_RESET = 0, 128, 256, 384
C_HEAD = C_RESET + T
C_ONES = C_HEAD + FOX_HEADS
C_ALL = C_ONES + P
G_NORM0, G_KV, G_NORM1, G_FIN, B_GATE, G_HEAD, B_F, V_ALL = 0, 8, 16, 24, 32, 40, 44, 45


def blk(b):
    return (0, META) if b == 0 else (META + (b - 1) * BLK, BLK)


class Shared:
    pass


class Steps:

    def __init__(self, sem, names, start=0):
        self.sem, self.names, self.n, self.start = sem, names, 0, start * len(names)
        self.index = {x: i for i, x in enumerate(names)}
        assert len(self.index) == len(names)

    def inc(self, name):
        want = self.names[self.n % len(self.names)]
        assert want == name, (want, name)
        self.n += 1
        return 1

    def so_far(self, it):
        return it * len(self.names) + (self.start + self.n % len(self.names))

    def at(self, it, name):
        return it * len(self.names) + (self.start + self.index[name] + 1)


def wait_for(eng, it, *steps):
    latest = {}
    for who, name, back in steps:
        value = who.index[name] - back * len(who.names)
        if id(who) not in latest or latest[id(who)][0] < value:
            latest[id(who)] = (value, who, name, back)
    for _, who, name, back in latest.values():
        eng.wait_ge(who.sem, who.at(it - back, name))


def turn(eng, steps, it):
    value = steps.so_far(it)
    if not (isinstance(value, int) and value == 0):
        eng.wait_ge(steps.sem, value)


def psum_views(psum):
    def bank(b, c0=0, c1=BANK, p0=0, p1=P):
        return psum[p0:p1, b * BANK + c0:b * BANK + c1]

    def halves(b, rows=P):
        return psum[0:rows, b * BANK:(b + 2) * BANK].rearrange("p (h n) -> p h n", h=2)[:, :, 0:HALF]

    def whole(b, rows=P):
        return psum[0:rows, (b + 1) * BANK - META:(b + 2) * BANK]

    return bank, halves, whole


def two(ap):
    return ap.rearrange("p (h n) -> p h n", h=2)


def project(nc, out, w_hi, w_lo, ktiles, x_hi, x_lo, before_k=None):
    last = None
    for k in ktiles:
        if before_k is not None:
            before_k(k)
        for w, x, n in ((w_hi, x_hi, 0), (w_hi, x_lo, 1), (w_lo, x_hi, 2)):
            for h in range(2):
                last = nc.tensor.matmul(out[:, h, :], w[:, k, :], x[:, k, h * HALF:(h + 1) * HALF],
                                        start=(k == ktiles[0] and n == 0), stop=(k == ktiles[-1] and n == 2))
    return last


def attend(nc, out, v_hi, v_lo, a_hi, a_lo):
    parts = ((v_hi, a_hi, 0), (v_hi, a_lo, 1), (v_lo, a_hi, 2))
    last = None
    for v, a, n in parts:
        last = nc.tensor.matmul(out[:, 0:META], v[0:META, 0, :], a[0:META, PK_META:PK_ALL], start=n == 0, stop=n == 2)
    for j in range(NBLK + 1):
        rows = blk(j)[1]
        for v, a, n in parts:
            last = nc.tensor.matmul(out[:, T - PK_W[j]:T], v[0:rows, j, :], a[0:rows, PK[j]:PK[j] + PK_W[j]],
                                    start=(j == 0 and n == 0), stop=(j == NBLK and n == 2))
    return last


def transpose_blocks(nc, main, meta, src, ident):
    last = None
    for b in range(NBLK + 1):
        t0, w = blk(b)
        dst = meta if b == 0 else main[:, t0:t0 + w]
        last = nc.tensor.transpose(dst, src[:, t0:t0 + w], ident)
    return last


def score_pieces(bank):
    return [(bank(4, 0, 512, 0, META), PK[0], 512, META), (bank(5), PK[1], 512, P), (bank(6, 0, 384), PK[2], 384, P),
            (bank(7, 0, 384), PK[3], 384, P), (bank(7, 384, 400, 0, META), PK_META, META, META)]


def norm_phase(nc, s, tag, gains, low=None, load=(), final_out=None):
    bank, halves, whole = psum_views(s.psum)
    with ExitStack() as c:
        sb = lambda name, shape, dt=F32: c.enter_context(nc.sbuf_tensor(f"{tag}_{name}", shape, dt))
        sem = lambda name: c.enter_context(nc.semaphore(f"{tag}_{name}"))
        loaded, stored = sem("loaded"), sem("stored")
        sq = sb("sq", [P, 2, T])
        acc = sb("acc", [P, T])
        rt = sb("rt", [P, T])
        xf = sb("xf", [P, 2, T])
        jobs = [(g, k) for g in range(len(gains)) for k in range(KT)]
        A = Steps(sem("act_done"), [f"sq{k}" for k in range(KT)] + ["sqrt"] + (["low_hi"] if low else [])
                  + ([f"hi{g}{k}" for g, k in jobs] if final_out is None else []))
        V = Steps(sem("dve_done"), ["eps"] + [f"acc{k}" for k in range(KT)] + ["rstd"] + (["low_lo"] if low else [])
                  + (["x00"] + [x for (g, k), (g1, k1) in zip(jobs, jobs[1:]) for x in (f"x{g1}{k1}", f"lo{g}{k}")]
                     + [f"lo{jobs[-1][0]}{KT - 1}"] if final_out is None else [f"x0{k}" for k in range(KT)]))
        E = Steps(sem("pe_done"), ["sum"] + (["low"] if low else []))
        if low:
            low_raw = sb("low_raw", [P, KT * RANK])
            low_hi = sb("low_hi", [P, KT, RANK], F32R)
            low_lo = sb("low_lo", [P, KT, RANK], F32R)
        n_loads = 16 * (len(load) + (1 if low else 0))
        block = c.enter_context(nc.Block())

        @block.sync
        def _(sp):
            for dst, src in load:
                sp.dma_start(dst, src).then_inc(loaded, 16)
            if low:
                sp.dma_start(low_raw[:], low).then_inc(loaded, 16)
            if final_out is not None:
                for k in range(KT):
                    sp.wait_ge(V.sem, V.at(0, f"x0{k}"))
                    sp.dma_start(final_out[:, k, :], s.hT[:, k, META:T]).then_inc(stored, 16)
                sp.wait_ge(stored, 16 * KT)

        @block.scalar
        def _(act):
            if n_loads:
                act.wait_ge(loaded, n_loads)
            for k in range(KT):
                if k >= 2:
                    act.wait_ge(V.sem, V.at(0, f"acc{k - 2}"))
                turn(act, A, 0)
                nc.scalar.activation(sq[:, k % 2, :], s.hT[:, k, :], ACT.Square).then_inc(A.sem, A.inc(f"sq{k}"))
            act.wait_ge(E.sem, E.at(0, "sum"))
            act.wait_ge(V.sem, V.at(0, "eps"))
            turn(act, A, 0)
            nc.scalar.activation(two(rt[:]), halves(4), ACT.Sqrt, scale=1.0 / D_MODEL, bias=s.eps[:]).then_inc(A.sem, A.inc("sqrt"))
            if low:
                turn(act, A, 0)
                nc.scalar.activation(low_hi[:].rearrange("p k n -> p (k n)"), low_raw[:], ACT.Copy).then_inc(A.sem, A.inc("low_hi"))
            if final_out is None:
                for n, (g, k) in enumerate(jobs):
                    act.wait_ge(V.sem, V.at(0, f"x{g}{k}"))
                    turn(act, A, 0)
                    nc.scalar.activation(gains[g][1][:, k, :], xf[:, n % 2, :], ACT.Copy).then_inc(A.sem, A.inc(f"hi{g}{k}"))

        @block.vector
        def _(dve):
            turn(dve, V, 0)
            nc.vector.memset(s.eps[:], EPS).then_inc(V.sem, V.inc("eps"))
            for k in range(KT):
                dve.wait_ge(A.sem, A.at(0, f"sq{k}"))
                if k == 0:
                    turn(dve, V, 0)
                    nc.vector.tensor_copy(acc[:], sq[:, 0, :]).then_inc(V.sem, V.inc("acc0"))
                else:
                    turn(dve, V, 0)
                    nc.vector.tensor_tensor(acc[:], acc[:], sq[:, k % 2, :], ALU.add).then_inc(V.sem, V.inc(f"acc{k}"))
            dve.wait_ge(A.sem, A.at(0, "sqrt"))
            turn(dve, V, 0)
            nc.vector.reciprocal(s.rstd[:], rt[:]).then_inc(V.sem, V.inc("rstd"))
            if low:
                dve.wait_ge(A.sem, A.at(0, "low_hi"))
                turn(dve, V, 0)
                nc.vector.tensor_tensor(low_lo[:].rearrange("p k n -> p (k n)"), low_raw[:],
                                        low_hi[:].rearrange("p k n -> p (k n)").bitcast(F32), ALU.subtract).then_inc(V.sem, V.inc("low_lo"))

            def low_part(n):
                g, k = jobs[n]
                dve.wait_ge(A.sem, A.at(0, f"hi{g}{k}"))
                turn(dve, V, 0)
                nc.vector.tensor_tensor(gains[g][2][:, k, :], xf[:, n % 2, :], gains[g][1][:, k, :].bitcast(F32),
                                        ALU.subtract).then_inc(V.sem, V.inc(f"lo{g}{k}"))

            for n, (g, k) in enumerate(jobs):
                dst = xf[:, n % 2, :] if final_out is None else s.hT[:, k, :]
                col = gains[g][0] + k
                turn(dve, V, 0)
                nc.vector.scalar_tensor_tensor(dst, s.hT[:, k, :], s.vec[:, col:col + 1], s.rstd[:],
                                               op0=ALU.mult, op1=ALU.mult).then_inc(V.sem, V.inc(f"x{g}{k}"))
                if final_out is None and n:
                    low_part(n - 1)
            if final_out is None:
                low_part(len(jobs) - 1)

        @block.tensor
        def _(pe):
            pe.wait_ge(V.sem, V.at(0, f"acc{KT - 1}"))
            for h in range(2):
                last = nc.tensor.matmul(halves(4)[:, h, :], s.ones, acc[:, h * HALF:(h + 1) * HALF], start=True, stop=True)
            last.then_inc(E.sem, E.inc("sum"))
            if low:
                pe.wait_ge(V.sem, V.at(0, "low_lo"))
                project(nc, halves(0, RANK), low_hi, low_lo, range(KT), gains[0][1], gains[0][2],
                        lambda k: pe.wait_ge(V.sem, V.at(0, f"lo0{k}"))).then_inc(E.sem, E.inc("low"))


def gla_layer(nc, s):
    bank, halves, whole = psum_views(s.psum)
    with ExitStack() as c:
        sb = lambda name, shape, dt=F32: c.enter_context(nc.sbuf_tensor(f"gla_{name}", shape, dt))
        sem = lambda name: c.enter_context(nc.semaphore(f"gla_{name}"))
        raw = sb("raw", [P, 2, CH])
        w_hi = sb("w_hi", [P, GLA_RING, CH], F32R)
        w_lo = sb("w_lo", [P, GLA_RING, CH], F32R)
        q = sb("q", [P, CT, T])
        k_ = sb("k", [P, CT, T])
        b_ = sb("b", [P, CT, T])
        s1 = sb("s1", [P, CT, T])
        s2 = sb("s2", [P, CT, T])
        qj = sb("qj", [P, CT, 10 * BLK])
        kb = sb("kb", [P, CT, META + 3 * BLK])
        qd = sb("qd", [P, CT, SEQ])
        kd = sb("kd", [P, CT, SEQ])
        q32 = sb("q32", [P, CT, SEQ // 64, 32])
        k32 = sb("k32", [P, CT, SEQ // 64, 32])
        q64 = sb("q64", [P, CT, NBLK, 64])
        k64 = sb("k64", [P, CT, NBLK, 64])
        qm = sb("qm", [P, CT, META])
        km = sb("km", [P, CT, META])
        eb = sb("eb", [P, CT, NBLK])
        a_hi = sb("a_hi", [P, PK_ALL], F32R)
        a_lo = sb("a_lo", [P, PK_ALL], F32R)
        vt = sb("vt", [P, T])
        v_hi = sb("v_hi", [P, 2, NBLK + 1, P], F32R)
        v_lo = sb("v_lo", [P, 2, NBLK + 1, P], F32R)
        sr = sb("sr", [P, 2, T])
        yf = sb("yf", [P, T])
        y_hi = sb("y_hi", [P, VT, T], F32R)
        y_lo = sb("y_lo", [P, VT, T], F32R)
        glow = sb("glow", [RANK, T])
        w_now = sb("w_now", [RANK, GLA_DK])
        sq = sb("sq", [P, T])
        acc = sb("acc", [P, T])
        zeros = sb("zeros", [P, P])
        start = sb("start", [P, 4])
        rt, wtmp = sq, yf
        qj_at = [0, 4 * BLK, 7 * BLK, 9 * BLK]

        raw_loaded = [sem("raw_loaded0"), sem("raw_loaded1")]
        hi_made, lo_made, glow_ready = sem("hi_made"), sem("lo_made"), sem("glow_ready")
        NC, NV = len(GLA_CHUNKS), GLA_HEADS
        A = Steps(sem("act_done"),
                  ["Wup", "G0", "G1", "Gexp", "Gln", "Q0", "Xqd", "Xkd", "Xq32", "Xk32", "Q1", "Xq64", "Xk64", "Xkb", "Xqb", "Xeb",
                   "Xqm", "Xkm", "K0", "K1", "V0", "R0", "X0", "V1", "R1", "S0", "S1", "S2", "S3", "S4", "X1", "V2",
                   "A0", "Y0", "R2", "A1", "Y1", "X2", "V3", "A2", "Y2", "X3", "R3", "A3", "Y3", "sqrt"], 1)
        V = Steps(sem("dve_done"),
                  ["G0", "G1", "Gla", "Gb0", "Gb1", "Dqd", "D32", "D64", "Dkb0", "Dkb", "Mqd", "Mq32", "Mq64", "Mqj0", "Mqj1",
                   "Mqj2", "Mqj3", "Mj2", "Mj1", "Mj0", "Mqm", "Mkd", "Mk32", "Mk64", "Mkb", "Mkm"]
                  + ["X0", "C1", "C2", "C3", "C4", "S0", "S1", "S2", "S3", "S4", "X1",
                     "A0", "Y0", "A1", "q1", "Y1", "X2", "A2", "q2", "Y2", "X3",
                     "A3", "q3", "Y3", "rstd"] + [x for d in range(KT) for x in (f"W{d}", f"H{d}")], 1)
        E = Steps(sem("pe_done"), GLA_JOBS[:11] + ["S"] + GLA_JOBS[11:22] + ["sum"] + GLA_JOBS[22:], 1)
        primes = [(A.sem, len(A.names)), (E.sem, len(E.names)), (lo_made, 2)]

        def frees(job):
            if job[0] in "QKVR":
                return A, job
            return V, job

        block = c.enter_context(nc.Block())

        @block.sync
        def _(sp):
            def load(it, c0, n):
                src = s.w_gla[bass.ds(it * NC + c0, 1)].rearrange("a p n -> p (a n)")
                sp.wait_ge(lo_made, n + 1)
                sp.dma_start(raw[:, c0 % 2, :], src).then_inc(raw_loaded[c0 % 2], 16)

            with sp.Fori(0, GLA_HEADS) as it:
                for c0 in range(NC):
                    load(it, c0, it * NC + c0)

        @block.scalar
        def _(act):
            def split(it, c0):
                act.wait_ge(raw_loaded[c0 % 2], it * (8 * NC) + 16 * (c0 // 2 + 1))
                if not (isinstance(it, int) and it == 0 and c0 < AHEAD):
                    before, back = (c0 - GLA_RING) % NC, it + (c0 - GLA_RING) // NC
                    job = GLA_CHUNKS[before]
                    job = f"W{int(job[1]) + 1}" if job[0] == "W" else job
                    act.wait_ge(E.sem, E.at(back, job))
                nc.scalar.activation(w_hi[:, c0 % GLA_RING, :], raw[:, c0 % 2, :], ACT.Copy).then_inc(hi_made, 1)

            def step(it, last):
                def ready(job):
                    if job in GLA_CHUNKS:
                        c0 = GLA_CHUNKS.index(job) + AHEAD
                        if c0 < NC or not last:
                            split(it, c0)
                    if job is not None and job[0] != "W":
                        act.wait_ge(E.sem, E.at(it, job))

                def act_op(name, out, in_, func, **kw):
                    turn(act, A, it)
                    nc.scalar.activation(out, in_, func, **kw).then_inc(A.sem, A.inc(name))

                act.wait_ge(E.sem, E.at(it - 1, "G1"))
                act_op("Wup", w_now[:], s.w_up[:, bass.ds(it * GLA_DK, GLA_DK)], ACT.Copy)
                for t in range(CT):
                    bias = s.vec[:, bass.ds(it * CT + (B_GATE + t), 1)]
                    ready(f"G{t}")
                    act_op(f"G{t}", two(s1[:, t, :]), halves(2 * t), ACT.Abs, bias=bias)
                act_op("Gexp", s1[:], s1[:], ACT.Exp, scale=-1.0)
                act_op("Gln", s1[:], s1[:], ACT.Ln, bias=1.0)
                ready("Q0")
                act_op("Q0", two(q[:, 0, :]), halves(0), ACT.Copy, scale=GLA_Q_SCALE)
                act.wait_ge(V.sem, V.at(it, "Dqd"))
                act_op("Xqd", qd[:], s1[:, :, META:T], ACT.Exp, scale=1 / GATE_NORM)
                act_op("Xkd", kd[:], s1[:, :, META:T], ACT.Exp, scale=-1 / GATE_NORM)
                act.wait_ge(V.sem, V.at(it, "D32"))
                v = s2[:, :, META:T].rearrange("p t (a h n) -> p t a h n", h=2, n=32)
                turn(act, A, it)
                for t in range(CT):
                    i = nc.scalar.activation(q32[:, t], v[:, t, :, 1, :], ACT.Exp, scale=1 / GATE_NORM)
                i.then_inc(A.sem, A.inc("Xq32"))
                turn(act, A, it)
                for t in range(CT):
                    i = nc.scalar.activation(k32[:, t], v[:, t, :, 0, :], ACT.Exp, scale=-1 / GATE_NORM)
                i.then_inc(A.sem, A.inc("Xk32"))
                ready("Q1")
                act_op("Q1", two(q[:, 1, :]), halves(2), ACT.Copy, scale=GLA_Q_SCALE)
                act.wait_ge(V.sem, V.at(it, "D64"))
                v = s1[:, :, META:T].rearrange("p t (a h n) -> p t a h n", h=2, n=64)
                turn(act, A, it)
                for t in range(CT):
                    i = nc.scalar.activation(q64[:, t], v[:, t, :, 1, :], ACT.Exp, scale=1 / GATE_NORM)
                i.then_inc(A.sem, A.inc("Xq64"))
                turn(act, A, it)
                for t in range(CT):
                    i = nc.scalar.activation(k64[:, t], v[:, t, :, 0, :], ACT.Exp, scale=-1 / GATE_NORM)
                i.then_inc(A.sem, A.inc("Xk64"))
                act.wait_ge(V.sem, V.at(it, "Dkb"))
                act_op("Xkb", kb[:], s2[:, :, 0:META + 3 * BLK], ACT.Exp, scale=-1 / GATE_NORM)
                act_op("Xqb", s1[:, :, META:T], b_[:, :, META:T], ACT.Exp, scale=1 / GATE_NORM)
                act_op("Xeb", eb[:], b_[:, :, META + BLK - 1:T:BLK], ACT.Exp, scale=1 / GATE_NORM)
                act_op("Xqm", qm[:], b_[:, :, 0:META], ACT.Exp, scale=1 / GATE_NORM)
                act_op("Xkm", km[:], b_[:, :, 0:META], ACT.Exp, scale=-1 / GATE_NORM)
                for t in range(CT):
                    ready(f"K{t}")
                    act_op(f"K{t}", two(k_[:, t, :]), halves(2 * t), ACT.Copy)

                def value(v):
                    slot = GLA_JOBS.index(f"V{v}") % 2
                    ready(f"V{v}")
                    act_op(f"V{v}", two(vt[:]), halves(2 * slot), ACT.Copy)

                def gate(v):
                    slot = GLA_JOBS.index(f"R{v}") % 2
                    ready(f"R{v}")
                    if v >= 2:
                        act.wait_ge(V.sem, V.at(it, f"A{v - 2}"))
                    act_op(f"R{v}", two(sr[:, v % 2, :]), halves(2 * slot), ACT.Silu)

                def values_hi(v):
                    slot = GLA_JOBS.index(f"X{v}") % 2
                    ready(f"X{v}")
                    turn(act, A, it)
                    nc.scalar.activation(v_hi[0:META, v % 2, 0, :], bank(2 * slot, 0, P, 0, META), ACT.Copy)
                    act_op(f"X{v}", v_hi[:, v % 2, 1:, :].rearrange("p b n -> p (b n)"), bank(2 * slot + 1), ACT.Copy)

                def attended(v):
                    slot = GLA_JOBS.index(f"A{v}") % 2
                    ready(f"A{v}")
                    if v >= 2:
                        act.wait_ge(V.sem, V.at(it, f"q{v - 1}"))
                    act_op(f"A{v}", (acc if v == 0 else sq)[:], whole(2 * slot), ACT.Square)
                    act.wait_ge(V.sem, V.at(it, f"A{v}"))
                    act_op(f"Y{v}", y_hi[:, v, :], yf[:], ACT.Copy)

                value(0)
                gate(0)
                values_hi(0)
                value(1)
                gate(1)
                ready("S")
                for n, (src, c0, w, rows) in enumerate(score_pieces(bank)):
                    if n:
                        act.wait_ge(V.sem, V.at(it, f"C{n}" if n < 3 else "C4"))
                    act_op(f"S{n}", a_hi[0:rows, c0:c0 + w], src, ACT.Copy)
                values_hi(1)
                value(2)
                attended(0)
                gate(2)
                attended(1)
                values_hi(2)
                value(3)
                attended(2)
                values_hi(3)
                gate(3)
                attended(3)
                ready("sum")
                act_op("sqrt", two(rt[:]), halves(4), ACT.Sqrt, scale=1.0 / GLA_DV, bias=s.eps[:])
                for d in range(0, KT, 2):
                    ready(f"W{d}")

            nc.scalar.activation(two(glow[:]), halves(0, RANK), ACT.Copy).then_inc(glow_ready, 1)
            for c0 in range(AHEAD):
                split(0, c0)
            with act.Fori(0, NV - 1) as it:
                step(it, False)
            step(NV - 1, True)

        @block.vector
        def _(dve):
            for i, (sm, n) in enumerate(primes):
                nc.vector.memset(start[:, i:i + 1], 0.0).then_inc(sm, n)
            nc.vector.memset(zeros[:], 0.0).then_inc(V.sem, len(V.names))

            def split(it, c0):
                dve.wait_ge(hi_made, it * NC + c0 + 1)
                nc.vector.tensor_tensor(w_lo[:, c0 % GLA_RING, :], raw[:, c0 % 2, :], w_hi[:, c0 % GLA_RING, :].bitcast(F32),
                                        ALU.subtract).then_inc(lo_made, 1)

            def step(it, last):
                def ready(job):
                    if job in GLA_CHUNKS:
                        c0 = GLA_CHUNKS.index(job) + AHEAD
                        if c0 < NC or not last:
                            split(it, c0)

                def tt(name, out, a, b, op):
                    turn(dve, V, it)
                    nc.vector.tensor_tensor(out, a, b, op).then_inc(V.sem, V.inc(name))

                for t in range(CT):
                    bias = s.vec[:, bass.ds(it * CT + (B_GATE + t), 1)]
                    dve.wait_ge(A.sem, A.at(it, f"G{t}"))
                    turn(dve, V, it)
                    nc.vector.tensor_scalar(two(s2[:, t, :]), halves(2 * t), bias, 0.0, ALU.add, ALU.min).then_inc(V.sem, V.inc(f"G{t}"))
                dve.wait_ge(A.sem, A.at(it, "Gln"))
                tt("Gla", s2[:], s2[:], s1[:], ALU.subtract)
                for t in range(CT):
                    turn(dve, V, it)
                    nc.vector.tensor_tensor_scan(b_[:, t, :], s.reset, s2[:, t, :], 0.0, ALU.mult, ALU.add).then_inc(V.sem, V.inc(f"Gb{t}"))
                bx = b_[:, :, META:T]

                def minus_at(name, out, width, mid):
                    x = bx.rearrange("p t (a n) -> p t a n", n=width)
                    ref = x[:, :, :, mid:mid + 1].to_broadcast([P, CT, SEQ // width, width])
                    turn(dve, V, it)
                    nc.vector.tensor_tensor(out[:, :, META:T].rearrange("p t (a n) -> p t a n", n=width), x, ref,
                                            ALU.subtract).then_inc(V.sem, V.inc(name))

                minus_at("Dqd", s1, 32, 15)
                minus_at("D32", s2, 64, 31)
                ready("Q0")
                dve.wait_ge(A.sem, A.at(it, "Xkd"))
                minus_at("D64", s1, 128, 63)
                dve.wait_ge(A.sem, A.at(it, "Xk32"))
                turn(dve, V, it)
                nc.vector.tensor_tensor(s2[:, :, 0:META], b_[:, :, 0:META], b_[:, :, META - 1:META].to_broadcast([P, CT, META]),
                                        ALU.subtract).then_inc(V.sem, V.inc("Dkb0"))
                minus_at("Dkb", s2, 128, 127)
                ready("Q1")
                dve.wait_ge(A.sem, A.at(it, "Q1"))
                qx = q[:, :, META:T]
                dve.wait_ge(A.sem, A.at(it, "Xqd"))
                tt("Mqd", qd[:], qd[:], qx, ALU.mult)
                dve.wait_ge(A.sem, A.at(it, "Xq32"))
                turn(dve, V, it)
                for t in range(CT):
                    i = nc.vector.tensor_tensor(q32[:, t], q32[:, t], qx[:, t].rearrange("p (a h n) -> p a h n", h=2, n=32)[:, :, 1, :], ALU.mult)
                i.then_inc(V.sem, V.inc("Mq32"))
                dve.wait_ge(A.sem, A.at(it, "Xq64"))
                turn(dve, V, it)
                for t in range(CT):
                    i = nc.vector.tensor_tensor(q64[:, t], q64[:, t], qx[:, t].rearrange("p (a h n) -> p a h n", h=2, n=64)[:, :, 1, :], ALU.mult)
                i.then_inc(V.sem, V.inc("Mq64"))
                dve.wait_ge(A.sem, A.at(it, "Xkm"))
                for j in range(NBLK):
                    cols = slice(j * BLK, (j + 1) * BLK)
                    tt(f"Mqj{j}", qj[:, :, qj_at[j]:qj_at[j] + BLK], s1[:, :, META:T][:, :, cols], qx[:, :, cols], ALU.mult)
                for j in range(NBLK - 2, -1, -1):
                    w = (NBLK - 1 - j) * BLK
                    tt(f"Mj{j}", qj[:, :, qj_at[j] + BLK:qj_at[j] + BLK + w], qj[:, :, qj_at[j + 1]:qj_at[j + 1] + w],
                       eb[:, :, j:j + 1].to_broadcast([P, CT, w]), ALU.mult)
                tt("Mqm", qm[:], qm[:], q[:, :, 0:META], ALU.mult)
                ready("K0")
                ready("K1")
                dve.wait_ge(A.sem, A.at(it, "K1"))
                kx = k_[:, :, META:T]
                tt("Mkd", kd[:], kd[:], kx, ALU.mult)
                turn(dve, V, it)
                for t in range(CT):
                    i = nc.vector.tensor_tensor(k32[:, t], k32[:, t], kx[:, t].rearrange("p (a h n) -> p a h n", h=2, n=32)[:, :, 0, :], ALU.mult)
                i.then_inc(V.sem, V.inc("Mk32"))
                turn(dve, V, it)
                for t in range(CT):
                    i = nc.vector.tensor_tensor(k64[:, t], k64[:, t], kx[:, t].rearrange("p (a h n) -> p a h n", h=2, n=64)[:, :, 0, :], ALU.mult)
                i.then_inc(V.sem, V.inc("Mk64"))
                tt("Mkb", kb[:], kb[:], k_[:, :, 0:META + 3 * BLK], ALU.mult)
                tt("Mkm", km[:], km[:], k_[:, :, 0:META], ALU.mult)

                def values_lo(v):
                    slot = GLA_JOBS.index(f"X{v}") % 2
                    dve.wait_ge(A.sem, A.at(it, f"X{v}"))
                    turn(dve, V, it)
                    nc.vector.tensor_tensor(v_lo[0:META, v % 2, 0, :], bank(2 * slot, 0, P, 0, META),
                                            v_hi[0:META, v % 2, 0, :].bitcast(F32), ALU.subtract)
                    tt(f"X{v}", v_lo[:, v % 2, 1:, :].rearrange("p b n -> p (b n)"), bank(2 * slot + 1),
                       v_hi[:, v % 2, 1:, :].rearrange("p b n -> p (b n)").bitcast(F32), ALU.subtract)

                def attended(v):
                    slot = GLA_JOBS.index(f"A{v}") % 2
                    dve.wait_ge(A.sem, A.at(it, f"A{v}"))
                    turn(dve, V, it)
                    nc.vector.scalar_tensor_tensor(yf[:], whole(2 * slot), s.vec[:, G_HEAD + v:G_HEAD + v + 1], sr[:, v % 2, :],
                                                   op0=ALU.mult, op1=ALU.mult).then_inc(V.sem, V.inc(f"A{v}"))
                    if v:
                        tt(f"q{v}", acc[:], acc[:], sq[:], ALU.add)
                    dve.wait_ge(A.sem, A.at(it, f"Y{v}"))
                    tt(f"Y{v}", y_lo[:, v, :], yf[:], y_hi[:, v, :].bitcast(F32), ALU.subtract)

                ready("V0")
                ready("R0")
                values_lo(0)
                ready("V1")
                ready("R1")
                dve.wait_ge(E.sem, E.at(it, "S"))
                turn(dve, V, it)
                nc.vector.memset(yf[:, 0:1], 0.0)
                for n, o in enumerate((bank(5, 0, BLK), bank(6, 0, BLK))):
                    nc.vector.copy_predicated(o, s.below, zeros[:]).then_inc(V.sem, V.inc(f"C{n + 1}"))
                nc.vector.copy_predicated(bank(7, 0, BLK), s.below, zeros[:])
                nc.vector.copy_predicated(bank(7, 256, 384), s.below, zeros[:]).then_inc(V.sem, V.inc("C3"))
                nc.vector.copy_predicated(bank(7, 384, 400, 0, META), s.below[0:META, 0:META], zeros[0:META, 0:META]).then_inc(V.sem, V.inc("C4"))
                for n, (src, c0, w, rows) in enumerate(score_pieces(bank)):
                    dve.wait_ge(A.sem, A.at(it, f"S{n}" if n < 3 else "S4"))
                    tt(f"S{n}", a_lo[0:rows, c0:c0 + w], src, a_hi[0:rows, c0:c0 + w].bitcast(F32), ALU.subtract)
                values_lo(1)
                ready("V2")
                attended(0)
                ready("R2")
                attended(1)
                values_lo(2)
                ready("V3")
                attended(2)
                values_lo(3)
                ready("R3")
                attended(3)
                dve.wait_ge(A.sem, A.at(it, "sqrt"))
                turn(dve, V, it)
                nc.vector.reciprocal(s.rstd[:], rt[:]).then_inc(V.sem, V.inc("rstd"))
                for d in range(KT):
                    slot = GLA_JOBS.index(f"W{d}") % 2
                    ready(f"W{d}")
                    dve.wait_ge(E.sem, E.at(it, f"W{d}"))
                    tt(f"W{d}", two(wtmp[:]), halves(2 * slot), two(s.rstd[:]), ALU.mult)
                    tt(f"H{d}", s.hT[:, d, :], s.hT[:, d, :], wtmp[:], ALU.add)

            for c0 in range(AHEAD):
                split(0, c0)
            with dve.Fori(0, NV - 1) as it:
                step(it, False)
            step(NV - 1, True)

        @block.tensor
        def _(pe):
            def step(it):
                def free(job, *steps):
                    n = GLA_JOBS.index(job)
                    wait_for(pe, it, (*frees(GLA_JOBS[n - 2]), int(n < 2)), *steps)
                    return n % 2

                def chunk(job):
                    c0 = GLA_CHUNKS.index(job)
                    pe.wait_ge(lo_made, it * NC + c0 + 3)
                    return c0 % GLA_RING

                def strip(job):
                    r = chunk(job)
                    slot = free(job)
                    w = [x[:, r, :].rearrange("p (k n) -> p k n", n=P) for x in (w_hi, w_lo)]
                    i = project(nc, halves(2 * slot), w[0], w[1], range(KT), s.xh, s.xl)
                    i.then_inc(E.sem, E.inc(job))

                def values(v):
                    slot = free(f"X{v}", (A, f"V{v}", 0))
                    transpose_blocks(nc, whole(2 * slot), bank(2 * slot, 0, P, 0, META), vt, s.ident).then_inc(E.sem, E.inc(f"X{v}"))

                def attention(v):
                    slot = free(f"A{v}", (V, f"X{v}", 0), (V, "S4", 0))
                    attend(nc, whole(2 * slot), v_hi[:, v % 2], v_lo[:, v % 2], a_hi, a_lo).then_inc(E.sem, E.inc(f"A{v}"))

                def scores():
                    pe.wait_ge(V.sem, V.at(it, "Mkm"))
                    def mm(out, lhs, rhs):
                        for t in range(CT):
                            i = nc.tensor.matmul(out, lhs[:, t], rhs[:, t], start=t == 0, stop=t == CT - 1)
                        return i
                    mm(bank(4, 0, 512, 0, META), kb[:, :, 0:META], qj[:, :, 0:4 * BLK])
                    for j, (bk, c0) in ((1, (5, BLK)), (2, (6, BLK)), (3, (7, BLK))):
                        w = (NBLK - j) * BLK
                        t0 = blk(j)[0]
                        mm(bank(bk, c0, c0 + w), kb[:, :, t0:t0 + BLK], qj[:, :, qj_at[j]:qj_at[j] + w])
                    for j, (bk, c0) in ((0, (5, 0)), (1, (6, 0)), (2, (7, 0)), (3, (7, 256))):
                        a = j * BLK
                        mm(bank(bk, c0 + 64, c0 + 128, 0, 64), k64[:, :, j, :], q64[:, :, j, :])
                        for u in range(2):
                            mm(bank(bk, c0 + 64 * u + 32, c0 + 64 * u + 64, 64 * u, 64 * u + 32), k32[:, :, 2 * j + u, :], q32[:, :, 2 * j + u, :])
                        for u in range(4):
                            x = slice(a + 32 * u, a + 32 * u + 32)
                            mm(bank(bk, c0 + 32 * u, c0 + 32 * u + 32, 32 * u, 32 * u + 32), kd[:, :, x], qd[:, :, x])
                    return mm(bank(7, 384, 400, 0, META), km, qm)

                for t in range(CT):
                    slot = free(f"G{t}", (A, "Wup", 0))
                    for h in range(2):
                        i = nc.tensor.matmul(halves(2 * slot)[:, h, :], w_now[:, t * P:(t + 1) * P], glow[:, h * HALF:(h + 1) * HALF],
                                             start=True, stop=True)
                    i.then_inc(E.sem, E.inc(f"G{t}"))
                for job in ("Q0", "Q1", "K0", "K1", "V0", "R0"):
                    strip(job)
                values(0)
                strip("V1")
                strip("R1")
                scores().then_inc(E.sem, E.inc("S"))
                values(1)
                strip("V2")
                attention(0)
                strip("R2")
                attention(1)
                values(2)
                strip("V3")
                attention(2)
                values(3)
                strip("R3")
                attention(3)
                wait_for(pe, it, (V, "q3", 0))
                for h in range(2):
                    i = nc.tensor.matmul(halves(4)[:, h, :], s.ones, acc[:, h * HALF:(h + 1) * HALF], start=True, stop=True)
                i.then_inc(E.sem, E.inc("sum"))
                for d in range(KT):
                    if d % 2 == 0:
                        r = chunk(f"W{d}")
                    slot = free(f"W{d}", (V, "Y3", 0))
                    w = [x[:, r, :].rearrange("p (k n) -> p k n", k=VT)[:, :, (d % 2) * P:(d % 2) * P + P] for x in (w_hi, w_lo)]
                    project(nc, halves(2 * slot), w[0], w[1], range(VT), y_hi, y_lo).then_inc(E.sem, E.inc(f"W{d}"))
            pe.wait_ge(glow_ready, 1)
            with pe.Fori(0, NV) as it:
                step(it)


def fox_layer(nc, s):
    bank, halves, whole = psum_views(s.psum)
    with ExitStack() as c:
        sb = lambda name, shape, dt=F32: c.enter_context(nc.sbuf_tensor(f"fox_{name}", shape, dt))
        sem = lambda name: c.enter_context(nc.semaphore(f"fox_{name}"))
        raw = sb("raw", [P, 2, CH])
        w_hi = sb("w_hi", [P, FOX_RING, CH], F32R)
        w_lo = sb("w_lo", [P, FOX_RING, CH], F32R)
        q_hi, q_lo = sb("q_hi", [P, T], F32R), sb("q_lo", [P, T], F32R)
        k_hi, k_lo = sb("k_hi", [P, T], F32R), sb("k_lo", [P, T], F32R)
        vt = sb("vt", [P, T])
        v_hi = sb("v_hi", [P, NBLK + 1, P], F32R)
        v_lo = sb("v_lo", [P, NBLK + 1, P], F32R)
        sr = sb("sr", [P, T])
        p_at = [0]
        for b in range(NBLK + 1):
            p_at.append(p_at[-1] + META + b * BLK)
        pr = sb("pr", [P, p_at[-1]])
        a_hi = sb("a_hi", [P, PK_ALL], F32R)
        a_lo = sb("a_lo", [P, PK_ALL], F32R)
        top_ = sb("top", [P, NBLK + 1])
        neg = sb("neg", [P, NBLK + 1])
        tot = sb("tot", [P, NBLK + 1])
        inv = sb("inv", [P, NBLK + 1])
        gate_all = sb("gate_all", [P, T])
        gate_q = sb("gate_q", [P, T], F32R)
        gate_k = sb("gate_k", [P, T], F32R)
        ident_r = sb("ident_r", [P, P], F32R)
        neg_r = sb("neg_r", [P, P], F32R)
        yf = sb("yf", [P, T])
        y_hi = sb("y_hi", [P, 2, T], F32R)
        y_lo = sb("y_lo", [P, 2, T], F32R)
        fa, fb, chi = yf, sr, vt

        raw_loaded = [sem("raw_loaded0"), sem("raw_loaded1")]
        hi_made, lo_made = sem("hi_made"), sem("lo_made")
        NC = len(FOX_CHUNKS)
        heads = range(2)
        blocks = range(NBLK + 1)
        AF = Steps(sem("gates_act"), ["abs", "exp", "ln", "chi", "chi_r", "ident", "neg"])
        VF = Steps(sem("gates_dve"), ["zero", "ones", "min", "log", "cum", "clo", "g0", "g32", "k64", "k96"])
        A = Steps(sem("act_done"),
                  ["K0", "Q0", "V0"] + [f"P0{b}" for b in blocks] + ["R0", "X0"] + [f"T0{n}" for n in range(5)]
                  + ["K1", "Q1"] + [f"P1{b}" for b in blocks] + ["Y0", "V1"] + [f"T1{n}" for n in range(5)] + ["X1", "R1", "Y1"], 1)
        def soft(a):
            return [f"L{a}"] + [x for b in blocks for x in (f"M{a}{b}", f"N{a}{b}")] + [x for b in blocks for x in (f"I{a}{b}", f"P{a}{b}")]
        V = Steps(sem("dve_done"),
                  ["K0", "Q0"] + soft(0) + ["X0"] + [f"T0{n}" for n in range(5)]
                  + ["K1", "Q1"] + soft(1) + ["A0", "Y0"] + [f"T1{n}" for n in range(5)] + ["X1", "A1", "Y1"]
                  + [f"W{d}" for d in range(KT)], 1)
        E = Steps(sem("pe_done"),
                  ["K0", "Q0", "V0"] + [f"S0{b}" for b in blocks] + ["R0", "X0", "T0", "K1", "Q1"] + [f"S1{b}" for b in blocks]
                  + ["A0", "V1", "T1", "X1", "R1", "A1"] + [f"W{d}" for d in range(KT)], 1)
        s_at = [(7, 0), (4, 0), (5, 0), (6, 0), (4, BANK - META)]

        def scores(b):
            bk, c0 = s_at[b]
            n = META + b * BLK
            return s.psum[0:blk(b)[1], bk * BANK + c0:bk * BANK + c0 + n]

        def frees(job):
            return (A, job) if job[0] in "VR" else (V, job)

        block = c.enter_context(nc.Block())

        @block.sync
        def _(sp):
            with sp.Fori(0, PAIRS) as it:
                for c0 in range(NC):
                    src = s.w_fox[bass.ds(it * NC + c0, 1)].rearrange("a p n -> p (a n)")
                    sp.wait_ge(lo_made, it * NC + c0 + 1)
                    sp.dma_start(raw[:, c0 % 2, :], src).then_inc(raw_loaded[c0 % 2], 16)

        @block.scalar
        def _(act):
            def split(it, c0):
                act.wait_ge(raw_loaded[c0 % 2], it * (8 * NC) + 16 * (c0 // 2 + 1))
                if not (isinstance(it, int) and it == 0 and c0 < AHEAD):
                    before, back = (c0 - FOX_RING) % NC, it + (c0 - FOX_RING) // NC
                    job = FOX_CHUNKS[before]
                    job = f"W{int(job[1]) + 3}" if job[0] == "W" else job
                    act.wait_ge(E.sem, E.at(back, job))
                nc.scalar.activation(w_hi[:, c0 % FOX_RING, :], raw[:, c0 % 2, :], ACT.Copy).then_inc(hi_made, 1)

            def step(it, last):
                def ready(job):
                    if job in FOX_CHUNKS:
                        c0 = FOX_CHUNKS.index(job) + AHEAD
                        if c0 < NC or not last:
                            split(it, c0)
                    if job[0] != "W":
                        act.wait_ge(E.sem, E.at(it, job))

                def slot(job):
                    return 2 * (FOX_JOBS.index(job) % 2)

                def act_op(name, out, in_, func, **kw):
                    turn(act, A, it)
                    nc.scalar.activation(out, in_, func, **kw).then_inc(A.sem, A.inc(name))

                def keys_queries(a):
                    ready(f"K{a}")
                    act_op(f"K{a}", two(k_hi[:]), halves(slot(f"K{a}")), ACT.Copy)
                    ready(f"Q{a}")
                    act_op(f"Q{a}", two(q_hi[:]), halves(slot(f"Q{a}")), ACT.Copy, scale=FOX_Q_SCALE)

                def value(a):
                    ready(f"V{a}")
                    act_op(f"V{a}", two(vt[:]), halves(slot(f"V{a}")), ACT.Copy)

                def softmax(a):
                    for b in blocks:
                        w = blk(b)[1]
                        act.wait_ge(V.sem, V.at(it, f"N{a}{b}"))
                        act_op(f"P{a}{b}", pr[0:w, p_at[b]:p_at[b + 1]], scores(b), ACT.Exp, bias=neg[0:w, b:b + 1],
                               accum_out=tot[0:w, b:b + 1])

                def gate(a):
                    ready(f"R{a}")
                    act_op(f"R{a}", two(sr[:]), halves(slot(f"R{a}")), ACT.Silu)

                def values_hi(a):
                    ready(f"X{a}")
                    x = slot(f"X{a}")
                    turn(act, A, it)
                    nc.scalar.activation(v_hi[0:META, 0, :], bank(x, 0, P, 0, META), ACT.Copy)
                    act_op(f"X{a}", v_hi[:, 1:, :].rearrange("p b n -> p (b n)"), bank(x + 1), ACT.Copy)

                def probs_hi(a):
                    ready(f"T{a}")
                    for n, (src, c0, w, rows) in enumerate(score_pieces(bank)):
                        act_op(f"T{a}{n}", a_hi[0:rows, c0:c0 + w], src, ACT.Copy)

                def attended(a):
                    act.wait_ge(V.sem, V.at(it, f"A{a}"))
                    act_op(f"Y{a}", y_hi[:, a, :], yf[:], ACT.Copy)

                keys_queries(0)
                value(0)
                softmax(0)
                gate(0)
                values_hi(0)
                probs_hi(0)
                keys_queries(1)
                softmax(1)
                attended(0)
                value(1)
                probs_hi(1)
                values_hi(1)
                gate(1)
                attended(1)
                ready("W0")
                ready("W4")

            turn(act, AF, 0)
            nc.scalar.activation(two(fa[0:FOX_HEADS, :]), halves(0, FOX_HEADS), ACT.Abs,
                                 bias=s.vec[0:FOX_HEADS, B_F:B_F + 1]).then_inc(AF.sem, AF.inc("abs"))
            turn(act, AF, 0)
            nc.scalar.activation(fa[0:FOX_HEADS, :], fa[0:FOX_HEADS, :], ACT.Exp, scale=-1.0).then_inc(AF.sem, AF.inc("exp"))
            turn(act, AF, 0)
            nc.scalar.activation(fa[0:FOX_HEADS, :], fa[0:FOX_HEADS, :], ACT.Ln, bias=1.0).then_inc(AF.sem, AF.inc("ln"))
            act.wait_ge(VF.sem, VF.at(0, "cum"))
            turn(act, AF, 0)
            nc.scalar.activation(gate_q[0:FOX_HEADS, :], fb[0:FOX_HEADS, :], ACT.Copy).then_inc(AF.sem, AF.inc("chi"))
            turn(act, AF, 0)
            nc.scalar.activation(chi[0:FOX_HEADS, :], gate_q[0:FOX_HEADS, :].bitcast(F32), ACT.Copy).then_inc(AF.sem, AF.inc("chi_r"))
            turn(act, AF, 0)
            nc.scalar.activation(ident_r[:], s.ident, ACT.Copy).then_inc(AF.sem, AF.inc("ident"))
            turn(act, AF, 0)
            nc.scalar.activation(neg_r[:], s.negs, ACT.Copy).then_inc(AF.sem, AF.inc("neg"))
            for c0 in range(AHEAD):
                split(0, c0)
            with act.Fori(0, PAIRS - 1) as it:
                step(it, False)
            step(PAIRS - 1, True)

        @block.vector
        def _(dve):
            for i, (sm, n) in enumerate(((A.sem, len(A.names)), (V.sem, len(V.names)), (E.sem, len(E.names)), (lo_made, 2))):
                nc.vector.memset(inv[:, i:i + 1], 0.0).then_inc(sm, n)

            def split(it, c0):
                dve.wait_ge(hi_made, it * NC + c0 + 1)
                nc.vector.tensor_tensor(w_lo[:, c0 % FOX_RING, :], raw[:, c0 % 2, :], w_hi[:, c0 % FOX_RING, :].bitcast(F32),
                                        ALU.subtract).then_inc(lo_made, 1)

            def step(it, last):
                def ready(job):
                    if job in FOX_CHUNKS:
                        c0 = FOX_CHUNKS.index(job) + AHEAD
                        if c0 < NC or not last:
                            split(it, c0)

                def slot(job):
                    return 2 * (FOX_JOBS.index(job) % 2)

                def tt(name, out, a, b, op):
                    turn(dve, V, it)
                    nc.vector.tensor_tensor(out, a, b, op).then_inc(V.sem, V.inc(name))

                def keys_queries(a):
                    ready(f"K{a}")
                    dve.wait_ge(A.sem, A.at(it, f"K{a}"))
                    tt(f"K{a}", two(k_lo[:]), halves(slot(f"K{a}")), two(k_hi[:].bitcast(F32)), ALU.subtract)
                    ready(f"Q{a}")
                    dve.wait_ge(A.sem, A.at(it, f"Q{a}"))
                    turn(dve, V, it)
                    nc.vector.scalar_tensor_tensor(two(q_lo[:]), halves(slot(f"Q{a}")), FOX_Q_SCALE, two(q_hi[:].bitcast(F32)),
                                                   op0=ALU.mult, op1=ALU.subtract).then_inc(V.sem, V.inc(f"Q{a}"))

                def softmax(a):
                    col = it * 2 + a
                    turn(dve, V, it)
                    nc.vector.tensor_scalar(gate_q[:], gate_all[:], s.head_rows(col), None, ALU.mult).then_inc(V.sem, V.inc(f"L{a}"))
                    for b in blocks:
                        w = blk(b)[1]
                        dve.wait_ge(E.sem, E.at(it, f"S{a}{b}"))
                        turn(dve, V, it)
                        nc.vector.reduce_max(top_[0:w, b:b + 1], scores(b), AX.X).then_inc(V.sem, V.inc(f"M{a}{b}"))
                        turn(dve, V, it)
                        nc.vector.tensor_scalar(neg[0:w, b:b + 1], top_[0:w, b:b + 1], -1.0, None, ALU.mult).then_inc(V.sem, V.inc(f"N{a}{b}"))
                    for b in blocks:
                        w = blk(b)[1]
                        x = pr[0:w, p_at[b]:p_at[b + 1]]
                        dve.wait_ge(A.sem, A.at(it, f"P{a}{b}"))
                        turn(dve, V, it)
                        nc.vector.reciprocal(inv[0:w, b:b + 1], tot[0:w, b:b + 1]).then_inc(V.sem, V.inc(f"I{a}{b}"))
                        turn(dve, V, it)
                        nc.vector.tensor_scalar(x, x, inv[0:w, b:b + 1], None, ALU.mult).then_inc(V.sem, V.inc(f"P{a}{b}"))

                def values_lo(a):
                    dve.wait_ge(A.sem, A.at(it, f"X{a}"))
                    x = slot(f"X{a}")
                    turn(dve, V, it)
                    nc.vector.tensor_tensor(v_lo[0:META, 0, :], bank(x, 0, P, 0, META), v_hi[0:META, 0, :].bitcast(F32), ALU.subtract)
                    tt(f"X{a}", v_lo[:, 1:, :].rearrange("p b n -> p (b n)"), bank(x + 1),
                       v_hi[:, 1:, :].rearrange("p b n -> p (b n)").bitcast(F32), ALU.subtract)

                def probs_lo(a):
                    for n, (src, c0, w, rows) in enumerate(score_pieces(bank)):
                        dve.wait_ge(A.sem, A.at(it, f"T{a}{n}" if n < 3 else f"T{a}4"))
                        tt(f"T{a}{n}", a_lo[0:rows, c0:c0 + w], src, a_hi[0:rows, c0:c0 + w].bitcast(F32), ALU.subtract)

                def attended(a):
                    dve.wait_ge(E.sem, E.at(it, f"A{a}"))
                    dve.wait_ge(A.sem, A.at(it, f"R{a}"))
                    tt(f"A{a}", yf[:], whole(slot(f"A{a}")), sr[:], ALU.mult)
                    dve.wait_ge(A.sem, A.at(it, f"Y{a}"))
                    tt(f"Y{a}", y_lo[:, a, :], yf[:], y_hi[:, a, :].bitcast(F32), ALU.subtract)

                keys_queries(0)
                ready("V0")
                softmax(0)
                ready("R0")
                values_lo(0)
                probs_lo(0)
                keys_queries(1)
                softmax(1)
                attended(0)
                ready("V1")
                probs_lo(1)
                values_lo(1)
                ready("R1")
                attended(1)
                for d in range(KT):
                    ready(f"W{d}")
                    dve.wait_ge(E.sem, E.at(it, f"W{d}"))
                    tt(f"W{d}", two(s.hT[:, d, :]), halves(slot(f"W{d}")), two(s.hT[:, d, :]), ALU.add)

            H = FOX_HEADS
            turn(dve, VF, 0)
            nc.vector.memset(gate_all[0:64, :], 0.0)
            turn(dve, VF, 0)
            nc.vector.memset(gate_k[64:P, :].bitcast(F32), 0.0).then_inc(VF.sem, VF.inc("zero"))
            turn(dve, VF, 0)
            nc.vector.memset(gate_all[64:P, :], 1.0)
            turn(dve, VF, 0)
            nc.vector.memset(gate_k[0:64, :].bitcast(F32), 1.0).then_inc(VF.sem, VF.inc("ones"))
            dve.wait_ge(AF.sem, AF.at(0, "abs"))
            turn(dve, VF, 0)
            nc.vector.tensor_scalar(two(fb[0:H, :]), halves(0, H), s.vec[0:H, B_F:B_F + 1], 0.0, ALU.add, ALU.min).then_inc(VF.sem, VF.inc("min"))
            dve.wait_ge(AF.sem, AF.at(0, "ln"))
            turn(dve, VF, 0)
            nc.vector.tensor_tensor(fa[0:H, :], fb[0:H, :], fa[0:H, :], ALU.subtract).then_inc(VF.sem, VF.inc("log"))
            turn(dve, VF, 0)
            nc.vector.tensor_tensor_scan(fb[0:H, :], gate_k[0:H, :].bitcast(F32), fa[0:H, :], 0.0, ALU.mult, ALU.add).then_inc(VF.sem, VF.inc("cum"))
            dve.wait_ge(AF.sem, AF.at(0, "chi_r"))
            turn(dve, VF, 0)
            nc.vector.tensor_tensor(fa[0:H, :], fb[0:H, :], chi[0:H, :], ALU.subtract).then_inc(VF.sem, VF.inc("clo"))
            turn(dve, VF, 0)
            nc.vector.tensor_copy(gate_all[0:H, :], chi[0:H, :]).then_inc(VF.sem, VF.inc("g0"))
            turn(dve, VF, 0)
            nc.vector.tensor_copy(gate_all[32:32 + H, :], fa[0:H, :]).then_inc(VF.sem, VF.inc("g32"))
            turn(dve, VF, 0)
            nc.vector.tensor_scalar(gate_k[64:64 + H, :], chi[0:H, :], -1.0, None, ALU.mult).then_inc(VF.sem, VF.inc("k64"))
            turn(dve, VF, 0)
            nc.vector.tensor_scalar(gate_k[96:96 + H, :], fa[0:H, :], -1.0, None, ALU.mult).then_inc(VF.sem, VF.inc("k96"))
            for c0 in range(AHEAD):
                split(0, c0)
            with dve.Fori(0, PAIRS - 1) as it:
                step(it, False)
            step(PAIRS - 1, True)

        @block.tensor
        def _(pe):
            def step(it):
                def free(job, *steps):
                    n = FOX_JOBS.index(job)
                    wait_for(pe, it, (*frees(FOX_JOBS[n - 2]), int(n < 2)), *steps)
                    return 2 * (n % 2)

                def chunk(job):
                    c0 = FOX_CHUNKS.index(job)
                    pe.wait_ge(lo_made, it * NC + c0 + 3)
                    return c0 % FOX_RING

                def strip(job, x_hi, x_lo):
                    r = chunk(job)
                    out = halves(free(job))
                    w = [x[:, r, :].rearrange("p (k n) -> p k n", n=P) for x in (w_hi, w_lo)]
                    project(nc, out, w[0], w[1], range(KT), x_hi, x_lo).then_inc(E.sem, E.inc(job))

                def head_scores(a):
                    wait_for(pe, it, (V, f"Q{a}", 0), (V, f"L{a}", 0))
                    for b in blocks:
                        t0, w = blk(b)
                        if b == NBLK:
                            pe.wait_ge(A.sem, A.at(it, f"P{a}2"))
                        bk, c0 = s_at[b]
                        n = t0 + w
                        parts = [(0, n, bk, c0)] if b < NBLK else [(0, META, bk, c0), (META, n, bk + 1, 0)]
                        for k0, k1, bk, c0 in parts:
                            o = bank(bk, c0, c0 + k1 - k0, 0, w)
                            masked = k1 > t0
                            nc.tensor.matmul(o, q_hi[:, t0:t0 + w], k_hi[:, k0:k1], start=True, stop=False)
                            nc.tensor.matmul(o, q_hi[:, t0:t0 + w], k_lo[:, k0:k1], start=False, stop=False)
                            nc.tensor.matmul(o, q_lo[:, t0:t0 + w], k_hi[:, k0:k1], start=False, stop=False)
                            i = nc.tensor.matmul(o, gate_q[:, t0:t0 + w], gate_k[:, k0:k1], start=False, stop=not masked)
                            if masked:
                                i = nc.tensor.matmul(bank(bk, c0 + t0 - k0, c0 + t0 - k0 + w, 0, w), ident_r[0:w, 0:w], neg_r[0:w, 0:w],
                                                     start=False, stop=True)
                        i.then_inc(E.sem, E.inc(f"S{a}{b}"))

                def values(a):
                    x = free(f"X{a}", (A, f"V{a}", 0))
                    transpose_blocks(nc, whole(x), bank(x, 0, P, 0, META), vt, s.ident).then_inc(E.sem, E.inc(f"X{a}"))

                def transpose_probs(a):
                    pe.wait_ge(V.sem, V.at(it, f"P{a}{NBLK}"))
                    pieces = score_pieces(bank)
                    for b in range(1, NBLK + 1):
                        nc.tensor.transpose(pieces[0][0][:, (b - 1) * BLK:b * BLK], pr[:, p_at[b]:p_at[b] + META], s.ident)
                        for j in range(1, b + 1):
                            x = p_at[b] + blk(j)[0]
                            dst = pieces[min(j, 3)][0]
                            c0 = (b - j) * BLK + (PK_W[3] if j == 4 else 0)
                            nc.tensor.transpose(dst[:, c0:c0 + BLK], pr[:, x:x + BLK], s.ident)
                    nc.tensor.transpose(pieces[4][0], pr[0:META, 0:META], s.ident[0:META, 0:META]).then_inc(E.sem, E.inc(f"T{a}"))

                def attention(a):
                    out = whole(free(f"A{a}", (V, f"X{a}", 0), (V, f"T{a}4", 0)))
                    attend(nc, out, v_hi, v_lo, a_hi, a_lo).then_inc(E.sem, E.inc(f"A{a}"))

                strip("K0", s.xh, s.xl)
                strip("Q0", s.x2h, s.x2l)
                strip("V0", s.xh, s.xl)
                head_scores(0)
                strip("R0", s.x2h, s.x2l)
                values(0)
                transpose_probs(0)
                strip("K1", s.xh, s.xl)
                strip("Q1", s.x2h, s.x2l)
                head_scores(1)
                attention(0)
                strip("V1", s.xh, s.xl)
                transpose_probs(1)
                values(1)
                strip("R1", s.x2h, s.x2l)
                attention(1)
                for d in range(KT):
                    if d % 4 == 0:
                        r = chunk(f"W{d}")
                    out = halves(free(f"W{d}", (V, "Y1", 0)))
                    w = [x[:, r, :].rearrange("p (k n) -> p k n", k=2)[:, :, (d % 4) * P:(d % 4 + 1) * P] for x in (w_hi, w_lo)]
                    project(nc, out, w[0], w[1], range(2), y_hi, y_lo).then_inc(E.sem, E.inc(f"W{d}"))

            pe.wait_ge(AF.sem, AF.at(0, "neg"))
            pe.wait_ge(VF.sem, VF.at(0, "k96"))
            with pe.Fori(0, PAIRS) as it:
                step(it)


def gla_fox_kernel(nc, xT, consts, vecs, w_low, w_up, w_gla, w_f, w_fox, out):
    with ExitStack() as c:
        sb = lambda name, shape, dt=F32: c.enter_context(nc.sbuf_tensor(name, shape, dt))
        psum = c.enter_context(nc.psum_tensor("psum", [P, 8 * BANK], F32))
        cst = sb("cst", [P, C_ALL])
        s = Shared()
        s.psum, s.w_gla, s.w_fox = psum, w_gla, w_fox
        s.vec = sb("vec", [P, V_ALL])
        s.hT = sb("hT", [P, KT, T])
        s.rstd = sb("rstd", [P, T])
        s.eps = sb("eps", [P, 1])
        s.xh = sb("xh", [P, KT, T], F32R)
        s.xl = sb("xl", [P, KT, T], F32R)
        s.ident = cst[:, C_IDENT:C_IDENT + P]
        s.below = cst[:, C_BELOW:C_BELOW + P].bitcast(I32)
        s.negs = cst[:, C_NEG:C_NEG + P]
        s.reset = cst[:, C_RESET:C_RESET + T]
        s.head_rows = lambda h: cst[:, bass.ds(h + C_HEAD, 1)]
        s.ones = cst[:, C_ONES:C_ONES + P]
        with ExitStack() as c2:
            s.w_up = c2.enter_context(nc.sbuf_tensor("w_up", [RANK, D_INNER // 2], F32))
            norm_phase(nc, s, "n1", [(G_NORM0, s.xh, s.xl)], low=w_low,
                       load=[(s.hT[:], xT), (cst[:], consts), (s.vec[:], vecs), (s.w_up[:], w_up)])
            gla_layer(nc, s)
        with ExitStack() as c3:
            s.x2h = c3.enter_context(nc.sbuf_tensor("x2h", [P, KT, T], F32R))
            s.x2l = c3.enter_context(nc.sbuf_tensor("x2l", [P, KT, T], F32R))
            norm_phase(nc, s, "n2", [(G_KV, s.xh, s.xl), (G_NORM1, s.x2h, s.x2l)], low=w_f)
            fox_layer(nc, s)
        norm_phase(nc, s, "n3", [(G_FIN, None, None)], final_out=out)


def kernel(x, meta_tokens, norm_g, gla_w_in, gla_w_gate_up, gla_b_gate, gla_head_norm_g, gla_w_out, kv_norm_g,
           fox_w_kv, fox_b_forget, fox_w_in, fox_w_out, final_norm_g):
    import numpy as np
    import concourse.bacc as bacc
    from concourse.bass_utils import run_bass_kernel_spmd

    def arr(a):
        return np.asarray(a)

    def cols(a):
        return arr(a).reshape(-1, P).T

    def strip(w, c0, n=P):
        return w[:, c0:c0 + n].reshape(KT, P, n).transpose(1, 0, 2).reshape(P, KT * n)

    def rows(w, r0, nk, c0, n):
        return w[r0:r0 + nk * P, c0:c0 + n].reshape(nk, P, n).transpose(1, 0, 2).reshape(P, nk * n)

    w1, wo1 = arr(gla_w_in)[0], arr(gla_w_out)[0]
    wkv, w2, wo2 = arr(fox_w_kv), arr(fox_w_in)[0], arr(fox_w_out)[0]
    half = D_INNER // 2
    o_k, o_v, o_low, o_r = half, 2 * half, 2 * half + D_INNER, 2 * half + D_INNER + RANK
    gla = []
    for h in range(GLA_HEADS):
        for name in GLA_CHUNKS:
            t = int(name[1])
            if name[0] == "W":
                gla.append(rows(wo1, h * GLA_DV, VT, t * P, 2 * P))
            else:
                base, n = {"Q": (0, CT), "K": (o_k, CT), "V": (o_v, VT), "R": (o_r, VT)}[name[0]]
                gla.append(strip(w1, base + (h * n + t) * P))
    fox = []
    for g in range(PAIRS):
        for name in FOX_CHUNKS:
            t = int(name[1])
            if name[0] == "W":
                fox.append(rows(wo2, g * 2 * P, 2, t * P, 4 * P))
            else:
                w, base = {"K": (wkv, 0), "V": (wkv, D_INNER), "Q": (w2, 0), "R": (w2, D_INNER)}[name[0]]
                fox.append(strip(w, base + (2 * g + t) * P))
    vec = np.zeros((P, V_ALL), np.float32)
    for at, a in ((G_NORM0, arr(norm_g)[0]), (G_KV, kv_norm_g), (G_NORM1, arr(norm_g)[1]), (G_FIN, final_norm_g),
                  (B_GATE, arr(gla_b_gate)[0]), (G_HEAD, arr(gla_head_norm_g)[0])):
        v = cols(a)
        vec[:, at:at + v.shape[1]] = v
    vec[0:FOX_HEADS, B_F] = arr(fox_b_forget)
    cst = np.zeros((P, C_ALL), np.float32)
    r = np.arange(P)
    cst[r, C_IDENT + r] = 1
    cst[:, C_BELOW:C_BELOW + P][r[:, None] > r[None, :]] = 1
    cst[:, C_NEG:C_NEG + P][r[:, None] < r[None, :]] = -1e30
    cst[:, C_RESET:C_RESET + T] = 1
    cst[:, [C_RESET + blk(b)[0] for b in range(NBLK + 1)]] = 0
    for h in range(FOX_HEADS):
        cst[r % 32 == h, C_HEAD + h] = 1
    cst[:, C_ONES:C_ONES + P] = 1
    tokens = np.concatenate([arr(meta_tokens), arr(x)[0]])
    ins = {
        "xT": tokens.T.reshape(KT, P, T).transpose(1, 0, 2),
        "consts": cst,
        "vecs": vec,
        "w_low": strip(w1, o_low, RANK),
        "w_up_": arr(gla_w_gate_up)[0],
        "w_gla": np.stack(gla),
        "w_f": strip(wkv, 2 * D_INNER, FOX_HEADS),
        "w_fox": np.stack(fox),
    }
    nc = bacc.Bacc("TRN2", target_bir_lowering=False, num_devices=1)
    ins = {k: np.ascontiguousarray(v) for k, v in ins.items()}
    aps = [nc.dram_tensor(k, v.shape, F32, kind="ExternalInput").ap() for k, v in ins.items()]
    out = nc.dram_tensor("outT", (P, KT, SEQ), F32, kind="ExternalOutput").ap()
    gla_fox_kernel(nc, *aps, out)
    res = run_bass_kernel_spmd(nc, [ins], core_ids=[0]).results[0]["outT"]
    return np.ascontiguousarray(res.reshape(P, KT, SEQ).transpose(2, 1, 0).reshape(1, SEQ, D_MODEL))
```
